# Optimizing a Trainium2 kernel written in Bass

```python
import jax, jax.numpy as jnp
from jax import lax
import numpy as np

D_MODEL = 1024
BATCH = 1
SEQ = 512
DEPTH = 1

CHUNK = 64
N_META = 16
CONV_WIDTH = D_MODEL // 2
CONV_K = 3
SB_HEADS = 8
SB_HEAD_DIM = 64
SB_WIDTH = SB_HEADS * SB_HEAD_DIM
Q_BLOCK = 128
PEER_HEADS = 8
PEER_N_KEYS = 128
PEER_N_EXPERTS = PEER_N_KEYS * PEER_N_KEYS
PEER_TOPK = 16
PEER_KEY_DIM = 256
PEER_HALF = PEER_KEY_DIM // 2
PEER_TOKEN_BLOCK = 128
IN_WIDTH = 3 * CONV_WIDTH + 3 * SB_WIDTH + 2 * D_MODEL
EPS = 1e-6

kernel_name = "hybrid_conv_stickbreak_peer_block"

def rmsnorm(x, g):
    xf = x.astype(jnp.float32)
    y = xf * lax.rsqrt(jnp.mean(xf * xf, axis=-1, keepdims=True) + EPS)
    return (y * g.astype(jnp.float32)).astype(x.dtype)

def causal_dwconv(u, w):
    k_width = w.shape[0]
    seq_len = u.shape[1]
    up = jnp.pad(u, ((0, 0), (k_width - 1, 0), (0, 0)))
    y = up[:, 0:seq_len] * w[0]
    for k in range(1, k_width):
        y = y + up[:, k:k + seq_len] * w[k]
    return y

def stick_breaking_attention(q, k, v):
    seq_len = q.shape[2]
    scale = q.shape[-1] ** -0.5
    outs = []
    for start in range(0, seq_len, Q_BLOCK):
        end = min(start + Q_BLOCK, seq_len)
        qb = q[:, :, start:end]
        kb = k[:, :, :end]
        vb = v[:, :, :end]
        z = jnp.einsum('bhqd,bhkd->bhqk', qb, kb).astype(jnp.float32) * scale
        t_pos = jnp.arange(start, end)[:, None]
        s_pos = jnp.arange(end)[None, :]
        past = s_pos < t_pos
        log_one_minus = jnp.where(past, jax.nn.log_sigmoid(-z), 0.0)
        suffix = lax.cumsum(log_one_minus, axis=3, reverse=True) - log_one_minus
        a = jnp.where(past, jnp.exp(jax.nn.log_sigmoid(z) + suffix), 0.0)
        outs.append(jnp.einsum('bhqk,bhkd->bhqd', a.astype(vb.dtype), vb))
    return jnp.concatenate(outs, axis=2)

def peer_layer(h, w_q, subkeys, u_tab, v_tab):
    bsz, seq_len, d = h.shape
    q = (h @ w_q).reshape(bsz, seq_len, PEER_HEADS, 2, PEER_HALF)
    s = jnp.einsum('blhpd,hpkd->blhpk', q, subkeys).astype(jnp.float32)
    s_top, i_top = lax.top_k(s, PEER_TOPK)
    cand = (s_top[..., 0, :, None] + s_top[..., 1, None, :]).reshape(
        bsz, seq_len, PEER_HEADS, PEER_TOPK * PEER_TOPK)
    score, ci = lax.top_k(cand, PEER_TOPK)
    i1 = jnp.take_along_axis(i_top[..., 0, :], ci // PEER_TOPK, axis=-1)
    i2 = jnp.take_along_axis(i_top[..., 1, :], ci % PEER_TOPK, axis=-1)
    idx = i1 * PEER_N_KEYS + i2
    gate = jax.nn.softmax(score, axis=-1)

    n_tok = bsz * seq_len
    n_sel = PEER_HEADS * PEER_TOPK
    pad = (-n_tok) % PEER_TOKEN_BLOCK
    hf = jnp.pad(h.reshape(n_tok, d), ((0, pad), (0, 0)))
    idf = jnp.pad(idx.reshape(n_tok, n_sel), ((0, pad), (0, 0)))
    gf = jnp.pad(gate.reshape(n_tok, n_sel).astype(h.dtype), ((0, pad), (0, 0)))
    n_blk = (n_tok + pad) // PEER_TOKEN_BLOCK
    hf = hf.reshape(n_blk, PEER_TOKEN_BLOCK, d)
    idf = idf.reshape(n_blk, PEER_TOKEN_BLOCK, n_sel)
    gf = gf.reshape(n_blk, PEER_TOKEN_BLOCK, n_sel)

    def expert_block(args):
        hb, ib, gb = args
        u = u_tab[ib]
        act = jax.nn.gelu(jnp.einsum('td,ted->te', hb, u))
        return jnp.einsum('te,ted->td', gb * act, v_tab[ib])

    y = lax.map(expert_block, (hf, idf, gf))
    return y.reshape(n_blk * PEER_TOKEN_BLOCK, d)[:n_tok].reshape(bsz, seq_len, d)

def setup_inputs(seed: int = 0) -> dict:
    key = jax.random.key(seed)
    ks = jax.random.split(key, 14)
    d = D_MODEL
    f32 = jnp.float32
    return {
        "x": jax.random.normal(ks[0], (BATCH, SEQ, d), f32),
        "meta": jax.random.normal(ks[1], (N_META, d), f32),
        "norm1_g": 1.0 + 0.05 * jax.random.normal(ks[2], (d,), f32),
        "w_in": jax.random.normal(ks[3], (d, IN_WIDTH), f32) * d ** -0.5,
        "conv_w": jax.random.normal(ks[4], (CONV_K, CONV_WIDTH), f32) * CONV_K ** -0.5,
        "w_branch_a": jax.random.normal(ks[5], (CONV_WIDTH, d), f32) * CONV_WIDTH ** -0.5,
        "w_branch_b": jax.random.normal(ks[6], (SB_WIDTH, d), f32) * SB_WIDTH ** -0.5,
        "w_out": jax.random.normal(ks[7], (d, d), f32) * d ** -0.5,
        "norm2_g": 1.0 + 0.05 * jax.random.normal(ks[8], (d,), f32),
        "peer_w_q": jax.random.normal(ks[9], (d, PEER_HEADS * PEER_KEY_DIM), f32) * d ** -0.5,
        "peer_subkeys": jax.random.normal(ks[10], (PEER_HEADS, 2, PEER_N_KEYS, PEER_HALF), f32) * PEER_HALF ** -0.5,
        "peer_u": jax.random.normal(ks[11], (PEER_N_EXPERTS, d), f32) * d ** -0.5,
        "peer_v": jax.random.normal(ks[12], (PEER_N_EXPERTS, d), f32) * 0.5,
        "final_g": 1.0 + 0.05 * jax.random.normal(ks[13], (d,), f32),
    }

def reference(x, meta, norm1_g, w_in, conv_w, w_branch_a, w_branch_b, w_out,
              norm2_g, peer_w_q, peer_subkeys, peer_u, peer_v, final_g):
    bsz = x.shape[0]
    meta_b = jnp.broadcast_to(meta.astype(x.dtype)[None], (bsz, N_META, D_MODEL))
    h_res = jnp.concatenate([meta_b, x], axis=1)
    seq_len = h_res.shape[1]

    for _ in range(DEPTH):
        h = rmsnorm(h_res, norm1_g)
        proj = h @ w_in
        c0 = 3 * CONV_WIDTH
        c1 = c0 + 3 * SB_WIDTH
        b_a, c_a, u_a = jnp.split(proj[..., :c0], 3, axis=-1)
        q, k, v = jnp.split(proj[..., c0:c1], 3, axis=-1)
        gate_a, gate_b = jnp.split(proj[..., c1:], 2, axis=-1)

        y_a = (b_a * causal_dwconv(c_a * u_a, conv_w)) @ w_branch_a

        def heads(t):
            return t.reshape(bsz, seq_len, SB_HEADS, SB_HEAD_DIM).transpose(0, 2, 1, 3)
        o = stick_breaking_attention(heads(q), heads(k), heads(v))
        o = o.transpose(0, 2, 1, 3).reshape(bsz, seq_len, SB_WIDTH)
        y_b = o @ w_branch_b

        mixed = jax.nn.sigmoid(gate_a) * y_a + jax.nn.sigmoid(gate_b) * y_b
        h_res = h_res + mixed @ w_out

        h2 = rmsnorm(h_res, norm2_g)
        h_res = h_res + peer_layer(h2, peer_w_q, peer_subkeys, peer_u, peer_v)

    out = rmsnorm(h_res, final_g)
    return out[:, N_META:]


_drawn_inputs = setup_inputs


def setup_inputs(seed=0):
    import zlib

    import numpy as np

    out = dict(_drawn_inputs(seed))
    spreads = {}
    factors = {}
    for name, (base, spread) in spreads.items():
        noise = np.random.default_rng([zlib.crc32(name.encode()), seed]).standard_normal(out[name].shape)
        drawn = base * np.exp(spread * noise) if base else spread * noise
        out[name] = __import__('jax').numpy.asarray(drawn.astype(out[name].dtype))
    for name, factor in factors.items():
        out[name] = (out[name] * factor).astype(out[name].dtype)
    return out
```

```python
from contextlib import ExitStack, contextmanager

import concourse.bass as bass
from concourse import mybir

F32 = mybir.dt.float32
U32 = mybir.dt.uint32
ALU = mybir.AluOpType
ACT = mybir.ActivationFunctionType
AX_X = mybir.AxisListType.X

P = 128
D = 1024
DC = D // P
SEQ = 512
TILES = SEQ // P
META = 16
PAD = P - META
CONV = 512
CC = CONV // P
PAIRS = 4
HEADS = 8
TOPK = 16
SEL = HEADS * TOPK
EPS = 1e-6
NEG = -3.0e38
GELU_A = 0.044715
GELU_B = 1.5957691216057308

UNIT_C, UNIT_G, UNIT_Q = 12, 16, 8
UNITS = UNIT_C + UNIT_G + UNIT_Q
WR = 4
TURNS = UNITS // WR
BATCH = 4
NBATCH = SEL // BATCH
RING = 2 * BATCH
WOVEN = 28
EARLY = NBATCH - WOVEN


class Chain:

    def __init__(self, eng, sem):
        self.eng, self.sem, self.base, self.k = eng, sem, 0, 0

    def link(self, ins):
        self.k += 1
        ins.then_inc(self.sem, 1)
        self.eng.wait_ge(self.sem, self.base + self.k)

    @contextmanager
    def loop(self, count, per):
        first = self.base + self.k
        with self.eng.Fori(0, count) as i:
            self.base, self.k = first + i * per, 0
            yield i
            assert self.k == per, f"{self.k} links in the loop's body"
        self.base, self.k = first + count * per, 0


def hybrid_block(nc, xT, x, g1, cw, g2, gf, sk, weights, table, out):
    with ExitStack() as ctx:
        def sb(name, shape, dt=F32):
            return ctx.enter_context(nc.sbuf_tensor(name, shape, dt))

        def sem(name):
            return ctx.enter_context(nc.semaphore(name))

        ident = sb("ident", [P, P])
        ones = sb("ones", [P, P])
        neg_ones = sb("neg_ones", [P, P])
        neg_tri = sb("neg_tri", [P, P])
        past = sb("past", [P, P])
        iota16 = sb("iota16", [P, TOPK])
        eps = sb("eps", [P, 1])
        g1_sb = sb("g1_sb", [P, DC])
        cw_sb = sb("cw_sb", [P, CC, 3])
        g2_b = sb("g2_b", [P, D])
        gf_b = sb("gf_b", [P, D])
        sk_sb = sb("sk_sb", [P, 2 * HEADS, P])
        wring = sb("wring", [P, WR, DC * 256])
        xt = sb("xt", [P, DC, 2 * P])
        hT = sb("hT", [P, DC, 2 * P])
        rstd = sb("rstd", [P, 2 * P])
        cs = sb("cs", [P, 2, 2 * (P + META)])
        cu = sb("cu", [P, CC, P + META + 2])
        bT = sb("bT", [P, CC, P])
        yaT = sb("yaT", [P, CC, P])
        kT = sb("kT", [P, PAIRS, (TILES + 1) * P])
        v = sb("v", [P, TILES + 1, 512])
        qT = sb("qT", [P, PAIRS, P])
        k_pair = sb("k_pair", [P, (TILES + 1) * P])
        v_pair = sb("v_pair", [P, TILES + 1, P])
        q_pair = sb("q_pair", [P, P])
        sp = sb("sp", [P, 2, (TILES + 1) * P])
        oT = sb("oT", [P, PAIRS, P])
        sg = sb("sg", [P, 4 * P])
        mixT = sb("mixT", [P, 2, P])
        x1 = sb("x1", [P, 2, D])
        h2 = sb("h2", [P, 2, D])
        ss2 = sb("ss2", [P, 2])
        rs2 = sb("rs2", [P, 2])
        qh = sb("qh", [P, 2 * P])
        tops = sb("tops", [P, 2, TOPK])
        topi = sb("topi", [P, 2, TOPK], U32)
        topf = sb("topf", [P, 2, TOPK])
        rest = sb("rest", [P, 2, P])
        cand = sb("cand", [P, TOPK * TOPK])
        cand2 = sb("cand2", [P, TOPK * TOPK])
        score = sb("score", [P, TOPK])
        ci = sb("ci", [P, TOPK], U32)
        cab = sb("cab", [P, 2, TOPK], U32)
        hit = sb("hit", [P, 2, TOPK, TOPK])
        picked = sb("picked", [P, 2, TOPK])
        nmax = sb("nmax", [P, 1])
        esc = sb("esc", [P, TOPK])
        esum = sb("esum", [P, 2])
        idx = sb("idx", [P, 2, SEL], U32)
        gate = sb("gate", [P, 2, SEL])
        rows = sb("rows", [P, RING, 2 * D])
        stage_idx = sb("stage_idx", [P, 2, BATCH], U32)
        act = sb("act", [P, 2, BATCH])
        g_arg = sb("g_arg", [P, 2, BATCH])
        g_exp = sb("g_exp", [P, 2, BATCH])
        coef = sb("coef", [P, 2, BATCH])
        diag = sb("diag", [P, RING, P])

        pf = ctx.enter_context(nc.psum_tensor("pf", [P, 4, 512], F32))
        px = ctx.enter_context(nc.psum_tensor("px", [P, D], F32))
        py = ctx.enter_context(nc.psum_tensor("py", [P, D], F32))

        s_const = sem("s_const")
        s_masks = sem("s_masks")
        s_fill = sem("s_fill")
        w_in = [sem(f"w_in{i}") for i in range(WR)]
        x_in = sem("x_in")
        res_in = sem("res_in")
        sq_ready = sem("sq_ready")
        ssum_mm = sem("ssum_mm")
        rstd_ready = sem("rstd_ready")
        h_ready = sem("h_ready")
        c_mm = sem("c_mm")
        c_ev = sem("c_ev")
        cu_done = sem("cu_done")
        conv_done = sem("conv_done")
        staged = sem("staged")
        z_mm = sem("z_mm")
        ln_ready = sem("ln_ready")
        sp_ready = sem("sp_ready")
        tri_mm = sem("tri_mm")
        mn_ready = sem("mn_ready")
        ex_ready = sem("ex_ready")
        at_ready = sem("at_ready")
        o_mm = sem("o_mm")
        o_ev = sem("o_ev")
        gate_mm = sem("gate_mm")
        ge_ready = sem("ge_ready")
        br_mm = sem("br_mm")
        mix_ready = sem("mix_ready")
        x1_mm = sem("x1_mm")
        rs2_ready = sem("rs2_ready")
        h2_ready = sem("h2_ready")
        tr_mm = sem("tr_mm")
        h2T_ready = sem("h2T_ready")
        q_mm = sem("q_mm")
        qh_ready = sem("qh_ready")
        sc_mm = sem("sc_mm")
        sc_used = sem("sc_used")
        nm_ready = sem("nm_ready")
        es_ready = sem("es_ready")
        idx_ready = sem("idx_ready")
        st_idx = sem("st_idx")
        row_in = [sem(f"row_in{i}") for i in range(RING)]
        arg_ready = sem("arg_ready")
        gexp_ready = sem("gexp_ready")
        coef_ready = sem("coef_ready")
        diag_ready = sem("diag_ready")
        v_done = sem("v_done")
        rs3_ready = sem("rs3_ready")
        out_ready = sem("out_ready")
        out_stored = sem("out_stored")
        dve_self = sem("dve_self")
        act_self = sem("act_self")

        def width(f):
            return P + META if f == 0 else P

        w_unit = [wring[:, s, :].rearrange("p (c n) -> p c n", c=DC) for s in range(WR)]
        w_out_unit = wring[:, 3, :].rearrange("p (c n) -> p c n", c=2)
        h2T = xt[:, :, 0:P]

        def weave(chain, f, batch, before, after, links):
            peer = f > 0
            first = EARLY if f == 1 else 0
            per = links["batch"] * peer

            def step(phase, b, u, *args):
                before.get(phase, nothing)(f, *args)
                if peer:
                    batch(f - 1, first + b, u)
                after.get(phase, nothing)(f, *args)

            step("head", 0, 0)
            for s in range(6):
                step("proj", 1 + s, (1 + s) % 2, 2 * s)
            with chain.loop(2, 2 * (links["attn"] + per)) as i:
                for s in range(2):
                    step("attn", 7 + 2 * i + s, (7 + s) % 2, 2 * i + s)
            before.get("prime", nothing)(f)
            with chain.loop(4, links["gates"] + 2 * per) as i:
                step("gates", 11 + 2 * i, 1, i)
                step("out", 12 + 2 * i, 0, i)
            step("norm", 19, 1)
            if peer:
                with chain.loop(2, 4 * (links["topk"] + per)) as i:
                    for s in range(4):
                        step("topk", 20 + 4 * i + s, s % 2, 4 * i + s, s, i)
            else:
                for s in range(4):
                    step("topk", 0, 0, s, s, 0)
                before.get("start", nothing)(0)
                for s in range(4):
                    before.get("topk", nothing)(0, 4 + s, s, 1)
                    batch(0, s, s % 2)
                    after.get("topk", nothing)(0, 4 + s, s, 1)

        def tail(chain, j, batch, links):
            first = {0: NBATCH, TILES - 1: 0}.get(j, WOVEN)
            if first < NBATCH:
                with chain.loop((NBATCH - first) // 2, 2 * links["batch"]) as i:
                    for u in range(2):
                        batch(j, first + 2 * i + u, u)

        def program(chain, batch, before, after, links):
            weave(chain, 0, batch, before, after, links)
            after.get("front", nothing)(0)
            for j in range(TILES):
                if j > 0:
                    before.get("start", nothing)(j)
                if j < TILES - 1:
                    weave(chain, j + 1, batch, before, after, links)
                    after.get("front", nothing)(j + 1)
                tail(chain, j, batch, links)
                after.get("tile", nothing)(j)

        def nothing(*_):
            pass

        block = ctx.enter_context(nc.Block())

        @block.sync
        def _(sp_q):
            sp_q.dma_start(xt[:, :, PAD:2 * P], xT[:, :, 0:P + META]).then_inc(x_in, 16)
            sp_q.dma_start(g1_sb[:], g1).then_inc(s_const, 16)
            sp_q.dma_start(cw_sb[:], cw).then_inc(s_const, 16)
            for s in range(WR):
                sp_q.dma_start(wring[:, s, :], weights[s]).then_inc(w_in[s], 16)
            sp_q.dma_start(g2_b[:], g2.partition_broadcast(P)).then_inc(s_const, 16)
            sp_q.dma_start(gf_b[:], gf.partition_broadcast(P)).then_inc(s_const, 16)
            sp_q.dma_start(sk_sb[:], sk).then_inc(s_const, 16)
            def turn(t, free):
                for s, (done, count) in enumerate(free):
                    sp_q.wait_ge(done, count)
                    unit = weights[t * WR + s] if isinstance(t, int) else \
                        weights[bass.ds(WR * t + s, 1)].rearrange("o p n -> (o p) n")
                    sp_q.dma_start(wring[:, s, :], unit).then_inc(w_in[s], 16)

            for f in range(TILES):
                if f > 0:
                    turn(0, [(q_mm, HEADS * f - WR + s + 1) for s in range(WR)])
                with sp_q.Fori(1, 4) as t:
                    turn(t, [(c_mm, UNIT_C * f - WR + s + 1 + t * WR) for s in range(WR)])
                with sp_q.Fori(4, 8) as t:
                    n = t + (4 * f - 3)
                    turn(t, [(gate_mm, n), (gate_mm, n), (br_mm, n), (x1_mm, n)])
                turn(8, [(q_mm, HEADS * f + s + 1) for s in range(WR)])

        @block.gpsimd
        def _(pool):
            pool.wait_ge(s_fill, 1)
            nc.gpsimd.affine_select(out=ident[:], in_=ones[:], compare_op=ALU.is_equal, fill=0.0, base=0,
                                    pattern=[[-1, P]], channel_multiplier=1)
            nc.gpsimd.affine_select(out=neg_tri[:], in_=neg_ones[:], compare_op=ALU.is_ge, fill=0.0, base=0,
                                    pattern=[[-1, P]], channel_multiplier=1)
            nc.gpsimd.affine_select(out=past[:], in_=ones[:], compare_op=ALU.is_gt, fill=0.0, base=0,
                                    pattern=[[1, P]], channel_multiplier=-1)
            nc.gpsimd.iota(iota16[:], pattern=[[1, TOPK]], base=0, channel_multiplier=0,
                           allow_small_or_imprecise_dtypes=True).then_inc(s_masks, 1)

            def gather(j, b, u):
                n = NBATCH * j + b
                for s in range(BATCH):
                    slot = BATCH * u + s
                    if not (isinstance(n, int) and n < 2):
                        pool.wait_ge(v_done, BATCH * n - RING + s + 1)
                        pool.nop(nofuse=True)
                    nc.gpsimd.tensor_copy(stage_idx[:, u, s:s + 1], idx[:, j % 2, bass.ds(BATCH * b + s, 1)]).then_inc(st_idx, 1)
                    pool.wait_ge(st_idx, BATCH * n + s + 1)
                    pool.nop(nofuse=True)
                    nc.gpsimd.indirect_dma_start(
                        out=rows[:, slot, :], out_offset=None, in_=table,
                        in_offset=bass.IndirectOffsetOnAxis(ap=stage_idx[:, u, s:s + 1], axis=0),
                    ).then_inc(row_in[slot], 16)

            per_head = TOPK // BATCH

            def head_rows(j, h):
                pool.wait_ge(idx_ready, HEADS * j + h + 1)
                for b in range(per_head):
                    gather(j, per_head * h + b, b % 2)

            for j in range(TILES):
                if j == 0:
                    head_rows(0, 0)
                with pool.Fori(1 if j == 0 else 0, HEADS) as h:
                    head_rows(j, h)

        @block.scalar
        def _(eng):
            chain = Chain(eng, act_self)
            link = chain.link

            def activation(*a, **k):
                return nc.scalar.activation(*a, **k)

            def copy(o, i):
                return activation(o, i, ACT.Copy)

            def rsqrt_mean(dst, tmp, src):
                link(activation(tmp, src, ACT.Ln, scale=1.0 / D, bias=eps[:]))
                return activation(dst, tmp, ACT.Exp, scale=-0.5)

            def square(f):
                lo = 2 * P - width(f)
                if f == 0:
                    eng.wait_ge(s_fill, 2)
                eng.wait_ge(x_in, 16 * (f + 1))
                if f > 0:
                    eng.wait_ge(gate_mm, 4 * f)
                activation(hT[:, :, lo:], xt[:, :, lo:], ACT.Square).then_inc(sq_ready, 1)

            def head_scale(f):
                lo = 2 * P - width(f)
                eng.wait_ge(ssum_mm, f + 1)
                rsqrt_mean(rstd[:, lo:], rstd[:, lo:], pf[:, 0, 0:width(f)]).then_inc(rstd_ready, 1)

            def proj_unit(f, u):
                n = width(f)
                bank = pf[:, u % 4, :]
                two = bank[:, 0:2 * n].rearrange("p (h n) -> p h n", h=2)
                if u == 0:
                    if f >= 2:
                        eng.wait_ge(out_stored, 16 * (f - 1))
                    eng.dma_start(x1[:, f % 2, :], x[P * f:P * (f + 1), :]).then_inc(res_in, 16)
                eng.wait_ge(c_mm, UNIT_C * f + u + 1)
                if u < 4:
                    if 4 * f + u >= 2:
                        eng.wait_ge(cu_done, 4 * f + u - 1)
                    ins = copy(cs[:, u % 2, 0:2 * n], bank[:, 0:2 * n])
                elif u < 6:
                    if u == 4 and f > 0:
                        eng.wait_ge(conv_done, f)
                    ins = copy(bT[:, 2 * (u - 4):2 * (u - 4) + 2, :], two[:, :, n - P:n])
                elif u < 8:
                    at = PAD if f == 0 else P * (f + 1)
                    ins = copy(kT[:, 2 * (u - 6):2 * (u - 6) + 2, at:at + n], two)
                elif u < 10:
                    cols = slice(256 * (u - 8), 256 * (u - 8) + 256)
                    if f == 0:
                        copy(v[:, 0, cols], bank[:, 256:512])
                    ins = copy(v[:, f + 1, cols], bank[:, 0:256])
                else:
                    ins = activation(qT[:, 2 * (u - 10):2 * (u - 10) + 2, :], two[:, :, n - P:n], ACT.Copy, scale=0.125)
                ins.then_inc(c_ev, 1)

            def proj(f, u):
                proj_unit(f, u)
                proj_unit(f, u + 1)

            def stage_pair(f, c):
                nk = f + 2
                eng.wait_ge(c_ev, UNIT_C * (f + 1))
                copy(k_pair[:, 0:nk * P], kT[:, bass.ds(c, 1), 0:nk * P].rearrange("p o n -> p (o n)"))
                copy(q_pair[:], qT[:, bass.ds(c, 1), :].rearrange("p o n -> p (o n)"))
                copy(v_pair[:, 0:nk, :], v[:, 0:nk, bass.ds(c * P, P)]).then_inc(staged, 1)

            def attn(f, c):
                nk = f + 2
                pair = PAIRS * f + c
                z = pf[:].rearrange("p (e b) n -> p e (b n)", e=2)
                for e in range(2):
                    n = 2 * pair + e + 1
                    s = sp[:, e, 0:nk * P]
                    eng.wait_ge(z_mm, n)
                    link(activation(s, z[:, e, 0:nk * P], ACT.Abs))
                    link(activation(s, s, ACT.Exp, scale=-1.0))
                    activation(s, s, ACT.Ln, bias=1.0).then_inc(ln_ready, 1)
                for e in range(2):
                    n = 2 * pair + e + 1
                    last = sp[:, e, (nk - 1) * P:nk * P]
                    eng.wait_ge(mn_ready, n)
                    activation(sp[:, e, 0:(nk - 1) * P], z[:, e, 0:(nk - 1) * P], ACT.Exp)
                    activation(last, last, ACT.Exp).then_inc(ex_ready, 1)
                eng.wait_ge(o_mm, pair + 1)
                copy(oT[:, bass.ds(c, 1), :].rearrange("p o n -> p (o n)"), px[:, 0:P]).then_inc(o_ev, 1)

            def gates(f, d):
                eng.wait_ge(gate_mm, 4 * f + d + 1)
                activation(sg[:], pf[:, 0, :], ACT.Exp, scale=-1.0).then_inc(ge_ready, 1)

            def norm(f):
                eng.wait_ge(x1_mm, 4 * (f + 1))
                copy(x1[:, f % 2, :], px[:])
                link(activation(h2[:, f % 2, :], px[:], ACT.Square, accum_out=ss2[:, 0:1]))
                rsqrt_mean(rs2[:, 0:1], ss2[:, 0:1], ss2[:, 0:1]).then_inc(rs2_ready, 1)

            def transposed(f):
                eng.wait_ge(tr_mm, f + 1)
                copy(h2T, pf[:, 0:2, :].rearrange("p b (c n) -> p (b c) n", n=P)).then_inc(h2T_ready, 1)

            def query(f, h, s, i):
                eng.wait_ge(q_mm, HEADS * f + h + 1)
                copy(qh[:], pf[:, 2, 0:256]).then_inc(qh_ready, 1)

            def softmax(f, h, s, i):
                n = HEADS * f + h + 1
                eng.wait_ge(nm_ready, n)
                activation(esc[:], score[:], ACT.Exp, bias=nmax[:], accum_out=esum[:, 0:1]).then_inc(es_ready, 1)

            def batch(j, b, u):
                n = NBATCH * j + b
                eng.wait_ge(arg_ready, n + 1)
                activation(g_exp[:, u, :], g_arg[:, u, :], ACT.Exp, scale=-GELU_B).then_inc(gexp_ready, 1)
                eng.wait_ge(coef_ready, n + 1)
                if not (isinstance(n, int) and n < 2):
                    eng.wait_ge(v_done, BATCH * n - BATCH)
                for s in range(BATCH):
                    activation(diag[:, BATCH * u + s, :], ident[:], ACT.Copy,
                               scale=coef[:, u, s:s + 1]).then_inc(diag_ready, 1)

            def end_tile(j):
                eng.wait_ge(v_done, SEL * (j + 1))
                link(activation(h2[:, j % 2, :], py[:], ACT.Square, accum_out=ss2[:, 1:2]))
                rsqrt_mean(rs2[:, 1:2], ss2[:, 1:2], ss2[:, 1:2]).then_inc(rs3_ready, 1)
                eng.wait_ge(out_ready, j + 1)
                eng.dma_start(out[P * j:P * (j + 1), :], x1[:, j % 2, :]).then_inc(out_stored, 16)

            def load_next(f):
                if f + 1 < TILES:
                    at = META + P * (f + 1)
                    eng.wait_ge(q_mm, HEADS * (f + 1))
                    eng.dma_start(xt[:, :, P:2 * P], xT[:, :, at:at + P]).then_inc(x_in, 16)

            nc.scalar.preload_act_table_set("natural_log_exp_and_others")
            eng.wait_ge(s_masks, 1)
            program(chain, batch,
                    before={"head": square, "attn": stage_pair, "norm": norm, "topk": query},
                    after={"head": head_scale, "proj": proj, "attn": attn, "gates": gates, "norm": transposed,
                           "topk": softmax, "front": load_next, "tile": end_tile},
                    links={"attn": 4, "batch": 0, "gates": 0, "topk": 0})
            eng.wait_ge(out_stored, 16 * TILES)

        @block.vector
        def _(eng):
            chain = Chain(eng, dve_self)
            link = chain.link
            dve = nc.vector

            def head(f):
                lo = 2 * P - width(f)
                eng.wait_ge(rstd_ready, f + 1)
                for c in range(DC):
                    ins = dve.scalar_tensor_tensor(out=hT[:, c, lo:], in0=xt[:, c, lo:], scalar=g1_sb[:, c:c + 1],
                                                   in1=rstd[:, lo:], op0=ALU.mult, op1=ALU.mult)
                ins.then_inc(h_ready, 1)

            def proj(f, u):
                proj_unit(f, u)
                proj_unit(f, u + 1)

            def proj_unit(f, u):
                n = width(f)
                if u < 4:
                    eng.wait_ge(c_ev, UNIT_C * f + u + 1)
                    dve.tensor_tensor(cu[:, u, 2:2 + n], cs[:, u % 2, 0:n], cs[:, u % 2, n:2 * n], ALU.mult).then_inc(cu_done, 1)
                elif u == 5:
                    eng.wait_ge(c_ev, UNIT_C * f + u + 1)
                    eng.wait_ge(cu_done, 4 * (f + 1))
                    off = n - P
                    for k in range(3):
                        for c in range(CC):
                            src = cu[:, c, off + k:off + k + P]
                            w = cw_sb[:, c, k:k + 1]
                            if k == 0:
                                ins = dve.tensor_scalar(yaT[:, c, :], src, w, None, ALU.mult)
                            else:
                                ins = dve.scalar_tensor_tensor(out=yaT[:, c, :], in0=src, scalar=w, in1=yaT[:, c, :],
                                                               op0=ALU.mult, op1=ALU.add)
                        link(ins)
                    dve.tensor_tensor(yaT[:], yaT[:], bT[:], ALU.mult).then_inc(conv_done, 1)
                    link(dve.tensor_copy(cu[:, :, 0:2], cu[:, :, n:n + 2]))

            def attn(f, c):
                nk = f + 2
                pair = PAIRS * f + c
                z = pf[:].rearrange("p (e b) n -> p e (b n)", e=2)
                for e in range(2):
                    last = sp[:, e, (nk - 1) * P:nk * P]
                    eng.wait_ge(ln_ready, 2 * pair + e + 1)
                    link(dve.scalar_tensor_tensor(out=sp[:, e, 0:nk * P], in0=z[:, e, 0:nk * P], scalar=0.0,
                                                  in1=sp[:, e, 0:nk * P], op0=ALU.max, op1=ALU.add))
                    dve.tensor_tensor(last, last, past[:], ALU.mult).then_inc(sp_ready, 1)
                for e in range(2):
                    last = sp[:, e, (nk - 1) * P:nk * P]
                    eng.wait_ge(tri_mm, 2 * pair + e + 1)
                    dve.tensor_scalar(last, z[:, e, (nk - 1) * P:nk * P], 0.0, None, ALU.min).then_inc(mn_ready, 1)
                for e in range(2):
                    last = sp[:, e, (nk - 1) * P:nk * P]
                    eng.wait_ge(ex_ready, 2 * pair + e + 1)
                    dve.tensor_tensor(last, last, past[:], ALU.mult).then_inc(at_ready, 1)

            def gates(f, d):
                n = 4 * f + d + 1
                eng.wait_ge(ge_ready, n)
                link(dve.tensor_scalar(sg[:], sg[:], 1.0, None, ALU.add))
                link(dve.reciprocal(sg[:], sg[:]))
                eng.wait_ge(br_mm, n)
                link(dve.tensor_tensor(sg[:], sg[:], pf[:, 1, :], ALU.mult))
                s4 = sg[:].rearrange("p (k g n) -> p k g n", k=2, g=2)
                dve.tensor_tensor(mixT[:], s4[:, :, 0, :], s4[:, :, 1, :], ALU.add).then_inc(mix_ready, 1)

            def norm(f):
                eng.wait_ge(rs2_ready, f + 1)
                if f == 0:
                    eng.wait_ge(s_const, 16 * 5)
                dve.scalar_tensor_tensor(out=h2[:, f % 2, :], in0=px[:], scalar=rs2[:, 0:1], in1=g2_b[:],
                                         op0=ALU.mult, op1=ALU.mult).then_inc(h2_ready, 1)

            def topk(f, h, s, i):
                n = HEADS * f + h + 1
                eng.wait_ge(sc_mm, n)
                eng.nop(nofuse=True)
                sc = pf[:, 3, 0:256].rearrange("p (t n) -> p t n", t=2)
                dve.max(tops[:, 0, 0:8], sc[:, 0, :])
                link(dve.max(tops[:, 1, 0:8], sc[:, 1, :]))
                eng.nop(nofuse=True)
                for t in range(2):
                    dve.max_index(topi[:, t, 0:8], tops[:, t, 0:8], sc[:, t, :])
                for t in range(2):
                    ins = dve.match_replace(rest[:, t, :], tops[:, t, 0:8], sc[:, t, :], NEG)
                ins.then_inc(sc_used, 1)
                eng.wait_ge(sc_used, n)
                eng.nop(nofuse=True)
                dve.max(tops[:, 0, 8:16], rest[:, 0, :])
                link(dve.max(tops[:, 1, 8:16], rest[:, 1, :]))
                eng.nop(nofuse=True)
                for t in range(2):
                    dve.max_index(topi[:, t, 8:16], tops[:, t, 8:16], rest[:, t, :])
                link(dve.tensor_tensor(cand[:].rearrange("p (a b) -> p a b", a=TOPK),
                                       tops[:, 0, :].unsqueeze(2).broadcast_to([P, TOPK, TOPK]),
                                       tops[:, 1, :].unsqueeze(1).broadcast_to([P, TOPK, TOPK]), ALU.add))
                dve.tensor_copy(topf[:], topi[:])
                link(dve.max(score[:, 0:8], cand[:]))
                dve.tensor_scalar(nmax[:], score[:, 0:1], -1.0, None, ALU.mult)
                dve.max_index(ci[:, 0:8], score[:, 0:8], cand[:])
                link(dve.match_replace(cand2[:], score[:, 0:8], cand[:], NEG))
                eng.nop(nofuse=True)
                dve.max(score[:, 8:16], cand2[:]).then_inc(nm_ready, 1)
                eng.wait_ge(nm_ready, n)
                eng.nop(nofuse=True)
                link(dve.max_index(ci[:, 8:16], score[:, 8:16], cand2[:]))
                dve.tensor_scalar(cab[:, 0, :], ci[:], 4, None, ALU.logical_shift_right)
                link(dve.tensor_scalar(cab[:, 1, :], ci[:], TOPK - 1, None, ALU.bitwise_and))
                link(dve.tensor_tensor(hit[:].rearrange("p t k j -> p (t k) j"),
                                       cab[:].rearrange("p t k -> p (t k)").unsqueeze(2).broadcast_to([P, 2 * TOPK, TOPK]),
                                       iota16[:].unsqueeze(1).broadcast_to([P, 2 * TOPK, TOPK]), ALU.is_equal))
                for t in range(2):
                    ins = dve.tensor_tensor(hit[:, t], hit[:, t], topf[:, t, :].unsqueeze(1).broadcast_to([P, TOPK, TOPK]), ALU.mult)
                link(ins)
                link(dve.tensor_reduce(picked[:], hit[:], AX_X, ALU.add))
                eng.wait_ge(es_ready, n)
                link(dve.reciprocal(esum[:, 1:2], esum[:, 0:1]))
                dve.tensor_scalar(gate[:, f % 2, bass.ds(TOPK * h, TOPK)], esc[:], esum[:, 1:2], None, ALU.mult)
                dve.scalar_tensor_tensor(out=idx[:, f % 2, bass.ds(TOPK * h, TOPK)], in0=picked[:, 0, :], scalar=128.0,
                                         in1=picked[:, 1, :], op0=ALU.mult, op1=ALU.add).then_inc(idx_ready, 1)

            def batch(j, b, u):
                n = NBATCH * j + b
                turn = (NBATCH // 2) * j + (b - u) // 2 if isinstance(b, int) else None
                for s in range(BATCH):
                    slot = BATCH * u + s
                    eng.wait_ge(row_in[slot], 16 * (turn + 1) if turn is not None else 8 * (n - u) + 16)
                    ins = dve.tensor_tensor_reduce(out=rows[:, slot, 0:D], in0=rows[:, slot, 0:D], in1=h2[:, j % 2, :],
                                                   scale=1.0, scalar=0.0, op0=ALU.mult, op1=ALU.add,
                                                   accum_out=act[:, u, s:s + 1])
                link(ins)
                a, arg, co = act[:, u, :], g_arg[:, u, :], coef[:, u, :]
                link(dve.tensor_tensor(arg, a, a, ALU.mult))
                link(dve.tensor_scalar(arg, arg, GELU_A, 1.0, ALU.mult, ALU.add))
                dve.tensor_tensor(arg, arg, a, ALU.mult).then_inc(arg_ready, 1)
                dve.tensor_tensor(a, a, gate[:, j % 2, bass.ds(BATCH * b, BATCH)], ALU.mult)
                eng.wait_ge(gexp_ready, n + 1)
                link(dve.tensor_scalar(co, g_exp[:, u, :], 1.0, None, ALU.add))
                link(dve.reciprocal(co, co))
                dve.tensor_tensor(co, co, a, ALU.mult).then_inc(coef_ready, 1)

            def end_tile(j):
                eng.wait_ge(rs3_ready, j + 1)
                dve.scalar_tensor_tensor(out=x1[:, j % 2, :], in0=py[:], scalar=rs2[:, 1:2], in1=gf_b[:],
                                         op0=ALU.mult, op1=ALU.mult).then_inc(out_ready, 1)

            dve.memset(neg_ones[:], -1.0)
            dve.memset(ones[:], 1.0).then_inc(s_fill, 1)
            dve.memset(eps[:], EPS)
            dve.memset(hT[:, :, 0:PAD], 0.0)
            dve.memset(kT[:, :, 0:PAD], 0.0)
            dve.memset(cu[:, :, 0:2], 0.0).then_inc(s_fill, 1)
            eng.wait_ge(s_fill, 2)
            eng.wait_ge(s_masks, 1)
            eng.wait_ge(s_const, 16 * 5)
            program(chain, batch,
                    before={"norm": norm},
                    after={"head": head, "proj": proj, "attn": attn, "gates": gates, "topk": topk, "tile": end_tile},
                    links={"attn": 2, "batch": 5, "gates": 3, "topk": 11})

        @block.tensor
        def _(eng):
            chain = Chain(eng, None)
            mm = nc.tensor.matmul

            def weight(f, u_slot, turn):
                eng.wait_ge(w_in[u_slot], 16 * (TURNS * f + turn + 1))

            def head(f):
                lo = 2 * P - width(f)
                eng.wait_ge(sq_ready, f + 1)
                for c in range(DC):
                    ins = mm(pf[:, 0, 0:width(f)], ones[:], hT[:, c, lo:], start=(c == 0), stop=(c == DC - 1))
                ins.then_inc(ssum_mm, 1)

            def proj(f, u):
                proj_unit(f, u)
                proj_unit(f, u + 1)

            def proj_unit(f, u):
                n = width(f)
                lo = 2 * P - n
                slot = u % WR
                if u == 0:
                    eng.wait_ge(h_ready, f + 1)
                    if f > 0:
                        eng.wait_ge(sc_used, HEADS * f)
                if u >= 4:
                    eng.wait_ge(c_ev, UNIT_C * f + u - 3)
                weight(f, slot, u // WR)
                if u in (8, 9):
                    for part in range(2 if f == 0 else 1):
                        for c in range(DC):
                            ins = mm(pf[:, slot, 256 * part:256 * part + 256],
                                     hT[:, c, P - P * part:2 * P - P * part], w_unit[slot][:, c, :],
                                     start=(c == 0), stop=(c == DC - 1))
                else:
                    for half in range(2):
                        for c in range(DC):
                            ins = mm(pf[:, slot, half * n:(half + 1) * n], w_unit[slot][:, c, half * P:(half + 1) * P],
                                     hT[:, c, lo:], start=(c == 0), stop=(c == DC - 1))
                ins.then_inc(c_mm, 1)

            def logits(f, c):
                nk = f + 2
                pair = PAIRS * f + c
                z = pf[:].rearrange("p (e b) n -> p e (b n)", e=2)
                eng.wait_ge(staged, pair + 1)
                for e in range(2):
                    r = slice(64 * e, 64 * e + 64)
                    for m in range(nk):
                        ins = mm(z[:, e, m * P:(m + 1) * P], k_pair[r, m * P:(m + 1) * P], q_pair[r, :],
                                 start=(m % 4 == 0), stop=False, skip_group_check=True)
                    ins.then_inc(z_mm, 1)

            def attn(f, c):
                nk = f + 2
                pair = PAIRS * f + c
                z = pf[:].rearrange("p (e b) n -> p e (b n)", e=2)
                for e in range(2):
                    eng.wait_ge(sp_ready, 2 * pair + e + 1)
                    for m in range(nk):
                        mm(z[:, e, m * P:(m + 1) * P], neg_tri[:], sp[:, e, m * P:(m + 1) * P],
                           start=False, stop=False, skip_group_check=True)
                    for m in range(1, nk):
                        src = sp[:, e, m * P:(m + 1) * P].unsqueeze(1).broadcast_to([P, m, P])
                        ins = mm(z[:, e, 0:m * P].rearrange("p (m n) -> p m n", n=P), neg_ones[:], src,
                                 start=False, stop=True, skip_group_check=True)
                    ins.then_inc(tri_mm, 1)
                for e in range(2):
                    r = slice(64 * e, 64 * e + 64)
                    eng.wait_ge(at_ready, 2 * pair + e + 1)
                    for m in range(nk):
                        ins = mm(px[r, 0:P], v_pair[:, m, r], sp[:, e, m * P:(m + 1) * P],
                                 start=(m == 0), stop=(m == nk - 1))
                ins.then_inc(o_mm, 1)

            def prime(f):
                eng.wait_ge(res_in, 16 * (f + 1))
                eng.wait_ge(o_ev, PAIRS * (f + 1))
                eng.wait_ge(conv_done, f + 1)
                for half in range(2):
                    mm(px[:, 512 * half:512 * half + 512], ident[:], x1[:, f % 2, 512 * half:512 * half + 512],
                       start=True, stop=False, skip_group_check=True)

            def gates(f, d):
                for k in range(2):
                    weight(f, k, 3 + d)
                    for half in range(2):
                        for c in range(DC):
                            ins = mm(pf[:, 0, (2 * k + half) * P:(2 * k + half + 1) * P],
                                     w_unit[k][:, c, half * P:(half + 1) * P], hT[:, c, P:],
                                     start=(c == 0), stop=(c == DC - 1))
                ins.then_inc(gate_mm, 1)
                weight(f, 2, 3 + d)
                for k in range(2):
                    for g, src in enumerate((yaT, oT)):
                        for c in range(CC):
                            ins = mm(pf[:, 1, (2 * k + g) * P:(2 * k + g + 1) * P],
                                     w_unit[2][:, CC * g + c, k * P:(k + 1) * P], src[:, c, :],
                                     start=(c == 0), stop=(c == CC - 1))
                ins.then_inc(br_mm, 1)

            def out_product(f, d):
                n = 4 * f + d + 1
                eng.wait_ge(mix_ready, n)
                weight(f, 3, 3 + d)
                for k in range(2):
                    for half in range(2):
                        ins = mm(px[:, 512 * half:512 * half + 512], mixT[:, k, :],
                                 w_out_unit[:, k, 512 * half:512 * half + 512],
                                 start=False, stop=False, skip_group_check=True)
                ins.then_inc(x1_mm, 1)

            def norm(f):
                eng.wait_ge(h2_ready, f + 1)
                for c in range(DC):
                    ins = nc.tensor.transpose(pf[:, c // 4, (c % 4) * P:(c % 4 + 1) * P], h2[:, f % 2, c * P:(c + 1) * P], ident[:])
                ins.then_inc(tr_mm, 1)

            def topk(f, h, s, i):
                n = HEADS * f + h + 1
                eng.wait_ge(h2T_ready, f + 1)
                weight(f, s, 7 + i)
                for t in range(2):
                    for c in range(DC):
                        ins = mm(pf[:, 2, t * P:(t + 1) * P], w_unit[s][:, c, t * P:(t + 1) * P], h2T[:, c, :],
                                 start=(c == 0), stop=(c == DC - 1))
                ins.then_inc(q_mm, 1)
                eng.wait_ge(qh_ready, n)
                if not (f == 0 and s == 0):
                    eng.wait_ge(sc_used, n - 1)
                elif True:
                    eng.wait_ge(sc_used, 4 * i)
                for t in range(2):
                    ins = mm(pf[:, 3, t * P:(t + 1) * P], qh[:, t * P:(t + 1) * P],
                             sk_sb[:, bass.ds(2 * h + t, 1), :].rearrange("p o n -> p (o n)"), start=True, stop=True)
                ins.then_inc(sc_mm, 1)

            def start_tile(j):
                eng.wait_ge(h2T_ready, j + 1)
                if j > 0:
                    eng.wait_ge(out_ready, j)
                for half in range(2):
                    mm(py[:, 512 * half:512 * half + 512], ident[:], x1[:, j % 2, 512 * half:512 * half + 512],
                       start=True, stop=False, skip_group_check=True)

            def batch(j, b, u):
                n = NBATCH * j + b
                for s in range(BATCH):
                    eng.wait_ge(diag_ready, BATCH * n + s + 1)
                    for half in range(2):
                        ins = mm(py[:, 512 * half:512 * half + 512], diag[:, BATCH * u + s, :],
                                 rows[:, BATCH * u + s, D + 512 * half:D + 512 * half + 512],
                                 start=False, stop=False, skip_group_check=True)
                    ins.then_inc(v_done, 1)

            eng.wait_ge(s_masks, 1)
            eng.wait_ge(s_fill, 2)
            eng.wait_ge(s_const, 16 * 5)
            program(chain, batch,
                    before={"head": head, "proj": proj, "attn": logits, "prime": prime, "gates": gates,
                            "out": out_product, "topk": topk, "start": start_tile},
                    after={"attn": attn, "norm": norm},
                    links={"attn": 0, "batch": 0, "gates": 0, "topk": 0})


def weight_units(np, w_in, w_branch_a, w_branch_b, w_out, w_q):
    def unit(w, *cols):
        return np.concatenate([w[:, a:b].reshape(-1, P, b - a) for a, b in cols], axis=2).transpose(1, 0, 2)

    units = [unit(w_in, (512 + P * i, 640 + P * i), (1024 + P * i, 1152 + P * i)) for i in range(4)]
    for at in (0, 2048, 2560, 1536):
        units += [unit(w_in, (at + 256 * i, at + 256 * i + 256)) for i in range(2)]
    for d in range(4):
        for k in range(2):
            at = P * (2 * d + k)
            units.append(unit(w_in, (3072 + at, 3072 + at + P), (4096 + at, 4096 + at + P)))
        cols = (256 * d, 256 * d + 256)
        units.append(np.concatenate([unit(w_branch_a, cols), unit(w_branch_b, cols)], axis=1))
        units.append(w_out[256 * d:256 * d + 256].reshape(2, P, D).transpose(1, 0, 2))
    units += [unit(w_q, (256 * h, 256 * h + 256)) for h in range(HEADS)]
    return np.ascontiguousarray(np.stack([u.reshape(P, 2048) for u in units]))


def kernel(**inputs):
    import numpy as np
    import concourse.bacc as bacc
    from concourse.bass_utils import run_bass_kernel_spmd

    a = {k: np.asarray(t) for k, t in inputs.items()}
    x = a["x"][0]
    tokens = np.concatenate([a["meta"], x], axis=0)
    arrays = {
        "xT": np.ascontiguousarray(tokens.T.reshape(DC, P, META + SEQ).transpose(1, 0, 2)),
        "x": np.ascontiguousarray(x),
        "g1": np.ascontiguousarray(a["norm1_g"].reshape(DC, P).T),
        "cw": np.ascontiguousarray(a["conv_w"].reshape(3, CC, P).transpose(2, 1, 0)),
        "g2": a["norm2_g"],
        "gf": a["final_g"],
        "sk": np.ascontiguousarray(a["peer_subkeys"].reshape(2 * HEADS, P, P).transpose(2, 0, 1)),
        "weights": weight_units(np, a["w_in"], a["w_branch_a"], a["w_branch_b"], a["w_out"], a["peer_w_q"]),
        "table": np.concatenate([a["peer_u"], a["peer_v"]], axis=1),
    }
    nc = bacc.Bacc("TRN2", target_bir_lowering=False, num_devices=1)
    aps = [nc.dram_tensor(k, t.shape, F32, kind="ExternalInput").ap() for k, t in arrays.items()]
    out = nc.dram_tensor("out", (SEQ, D), F32, kind="ExternalOutput").ap()
    hybrid_block(nc, *aps, out)
    r = run_bass_kernel_spmd(nc, [arrays], core_ids=[0])
    return r.results[0]["out"].reshape(1, SEQ, D)
```

```python
from contextlib import ExitStack, contextmanager

import concourse.bass as bass
from concourse import mybir

F32 = mybir.dt.float32
U32 = mybir.dt.uint32
ALU = mybir.AluOpType
ACT = mybir.ActivationFunctionType
AX_X = mybir.AxisListType.X

P = 128
D = 1024
DC = D // P
SEQ = 512
TILES = SEQ // P
META = 16
PAD = P - META
CONV = 512
CC = CONV // P
PAIRS = 4
HEADS = 8
TOPK = 16
SEL = HEADS * TOPK
EPS = 1e-6
NEG = -3.0e38
GELU_A = 0.044715
GELU_B = 1.5957691216057308

UNIT_C, UNIT_G, UNIT_Q = 12, 16, 8
WR = 4
TURN_C, TURN_G, TURN_Q = UNIT_C // WR, UNIT_G // WR, UNIT_Q // WR
GROUP = (TILES - 1) * P
SB_HEADS = 8
BATCH = 4
NBATCH = SEL // BATCH
RING = 2 * BATCH
WOVEN = 28
EARLY = NBATCH - WOVEN
FIRST_AT = 4
BY_DVE = {b: 4 if b < EARLY + 4 else 3 for b in range(EARLY, EARLY + 4 + 8)}


class Chain:

    def __init__(self, eng, sem):
        self.eng, self.sem, self.base, self.k = eng, sem, 0, 0

    def link(self, ins):
        self.k += 1
        ins.then_inc(self.sem, 1)
        self.eng.wait_ge(self.sem, self.base + self.k)

    @contextmanager
    def loop(self, count, per):
        first = self.base + self.k
        with self.eng.Fori(0, count) as i:
            self.base, self.k = first + i * per, 0
            yield i
            assert self.k == per, f"{self.k} links in the loop's body"
        self.base, self.k = first + count * per, 0


def hybrid_block(nc, xT, x, g1, cw, g2, gf, sk, weights, table, out):
    with ExitStack() as ctx:
        def sb(name, shape, dt=F32):
            return ctx.enter_context(nc.sbuf_tensor(name, shape, dt))

        def sem(name):
            return ctx.enter_context(nc.semaphore(name))

        ident = sb("ident", [P, P])
        ones = sb("ones", [P, P])
        neg_ones = sb("neg_ones", [P, P])
        neg_tri = sb("neg_tri", [P, P])
        past = sb("past", [P, P])
        iota16 = sb("iota16", [P, TOPK])
        eps = sb("eps", [P, 1])
        g1_sb = sb("g1_sb", [P, DC])
        cw_sb = sb("cw_sb", [P, CC, 3])
        g2_b = sb("g2_b", [P, D])
        gf_b = sb("gf_b", [P, D])
        sk_sb = sb("sk_sb", [P, 2 * HEADS, P])
        wring = sb("wring", [P, WR, DC * 256])
        hT = sb("hT", [P, DC, GROUP])
        rstd = sb("rstd", [P, GROUP])
        cs = sb("cs", [P, 2, 2, GROUP])
        cu = sb("cu", [P, GROUP + 2])
        carry = sb("carry", [P, CC, 2])
        yaT = sb("yaT", [P, CC, GROUP])
        kT = sb("kT", [P, PAIRS, (TILES + 1) * P])
        v = sb("v", [P, TILES + 1, 512])
        qT = sb("qT", [P, PAIRS, GROUP])
        sp = sb("sp", [P, 2, (TILES + 1) * P])
        oT = sb("oT", [P, PAIRS, P])
        sg = sb("sg", [P, 4 * P])
        mixT = sb("mixT", [P, 2, P])
        x1 = sb("x1", [P, 2, D])
        h2 = sb("h2", [P, 2, D])
        ss2 = sb("ss2", [P, 2])
        rs2 = sb("rs2", [P, 2])
        qh = sb("qh", [P, 2 * P])
        tops = sb("tops", [P, 2, TOPK])
        topi = sb("topi", [P, 2, TOPK], U32)
        topf = sb("topf", [P, 2, TOPK])
        rest = sb("rest", [P, 2, P])
        cand = sb("cand", [P, TOPK * TOPK])
        cand2 = sb("cand2", [P, TOPK * TOPK])
        score = sb("score", [P, TOPK])
        ci = sb("ci", [P, TOPK], U32)
        cab = sb("cab", [P, 2, TOPK], U32)
        hit = sb("hit", [P, 2, TOPK, TOPK])
        picked = sb("picked", [P, 2, TOPK])
        nmax = sb("nmax", [P, 1])
        esc = sb("esc", [P, TOPK])
        esum = sb("esum", [P, 2])
        idx = sb("idx", [P, 2, SEL], U32)
        gate = sb("gate", [P, 2, SEL])
        rows = sb("rows", [P, RING, 2 * D])
        stage_idx = sb("stage_idx", [P, 2, BATCH], U32)
        act = sb("act", [P, 2, BATCH])
        g_arg = sb("g_arg", [P, 2, BATCH])
        g_exp = sb("g_exp", [P, 2, BATCH])
        coef = sb("coef", [P, 2, BATCH])
        diag = sb("diag", [P, RING, P])

        pf = ctx.enter_context(nc.psum_tensor("pf", [P, 4, 512], F32))
        px = ctx.enter_context(nc.psum_tensor("px", [P, D], F32))
        py = ctx.enter_context(nc.psum_tensor("py", [P, D], F32))

        taps_in = sem("taps_in")
        s_const = sem("s_const")
        s_masks = sem("s_masks")
        s_fill = sem("s_fill")
        w_in = [sem(f"w_in{i}") for i in range(WR)]
        x_in = sem("x_in")
        res_in = sem("res_in")
        sq_ready = sem("sq_ready")
        ssum_mm = sem("ssum_mm")
        rstd_ready = sem("rstd_ready")
        h_ready = sem("h_ready")
        c_mm = sem("c_mm")
        c_ev = sem("c_ev")
        cs_used = sem("cs_used")
        conv_done = sem("conv_done")
        z_mm = sem("z_mm")
        ln_ready = sem("ln_ready")
        sp_ready = sem("sp_ready")
        tri_mm = sem("tri_mm")
        mn_ready = sem("mn_ready")
        ex_ready = sem("ex_ready")
        at_ready = sem("at_ready")
        o_mm = sem("o_mm")
        o_ev = sem("o_ev")
        gate_mm = sem("gate_mm")
        ge_ready = sem("ge_ready")
        br_mm = sem("br_mm")
        mix_ready = sem("mix_ready")
        x1_mm = sem("x1_mm")
        rs2_ready = sem("rs2_ready")
        h2_ready = sem("h2_ready")
        tr_mm = sem("tr_mm")
        h2T_ready = sem("h2T_ready")
        q_mm = sem("q_mm")
        qh_ready = sem("qh_ready")
        sc_mm = sem("sc_mm")
        sc_used = sem("sc_used")
        nm_ready = sem("nm_ready")
        es_ready = sem("es_ready")
        idx_ready = sem("idx_ready")
        st_idx = sem("st_idx")
        row_in = [sem(f"row_in{i}") for i in range(RING)]
        arg_ready = sem("arg_ready")
        gexp_ready = sem("gexp_ready")
        coef_ready = sem("coef_ready")
        diag_ready = sem("diag_ready")
        acc_done = sem("acc_done")
        v_done = sem("v_done")
        rs3_ready = sem("rs3_ready")
        out_ready = sem("out_ready")
        out_stored = sem("out_stored")
        dve_self = sem("dve_self")
        act_self = sem("act_self")

        def width(g):
            return P + META if g == 0 else GROUP

        def tokens(g):
            return P if g == 0 else GROUP

        def lo(g):
            return PAD if g == 0 else 0

        def col(f):
            return 0 if f == 0 else P * (f - 1)

        def h_tile(f):
            return hT[:, :, P:2 * P] if f == 0 else hT[:, :, col(f):col(f) + P]

        def first_turn(f):
            return (TURN_C + TURN_G + TURN_Q) * f if f < 2 else 2 * TURN_C + (TURN_G + TURN_Q) * f

        def gate_turn(f):
            return first_turn(f) + (TURN_C if f < 2 else 0)

        def by_dve(n):
            return BY_DVE.get(n, 0) if isinstance(n, int) else 0

        def by_dve_before(n):
            return sum(k for b, k in BY_DVE.items() if not isinstance(n, int) or b < n)

        def two_banks(u):
            b = 2 * (u % 2) if u < 6 else 0
            return pf[:, b:b + 2, :]

        acc = h2[:, 1, :]

        h2T = cs[:].rearrange("p a b n -> p (a b n)")[:, 0:D].rearrange("p (c n) -> p c n", c=DC)

        def logit_banks(f, h):
            e = h % 2
            return pf[:, 2 + e, :] if f < 2 else pf[:, 2 * e:2 * e + 2, :].rearrange("p b n -> p (b n)")

        w_unit = [wring[:, s, :].rearrange("p (c n) -> p c n", c=DC) for s in range(WR)]
        w_out_unit = wring[:, 3, :].rearrange("p (c n) -> p c n", c=2)

        def nothing(*_):
            pass

        def weave(chain, f, batch, before, after, links):
            peer = f > 0
            first = EARLY if f == 1 else 0
            per = links["batch"] * peer

            def step(phase, b, u, *args):
                before.get(phase, nothing)(f, *args)
                if peer:
                    batch(f - 1, first + b, u)
                after.get(phase, nothing)(f, *args)

            if f < 2:
                if f == 0:
                    before.get("head", nothing)(0)
                    after.get("head", nothing)(0)
                for b, units in enumerate(((0,), (1,), (2, 3), (4, 5))):
                    step("proj", b, b % 2, units)
                at, batches, units = 4, SB_HEADS, 6
            else:
                step("plain", 0, 0)
                at, batches, units = 1, SB_HEADS + 2, 0
            for n in range(SB_HEADS + 2):
                more = (6 + n,) if n < units else ()
                stages = [(h,) if 0 <= h < SB_HEADS else () for h in (n, n - 1, n - 2)]
                for phase, part in (("values", stages[2]), ("logits", stages[0]), ("proj", more)):
                    before.get(phase, nothing)(f, part)
                if peer and n < batches:
                    batch(f - 1, first + at + n, (at + n) % 2)
                for phase, part in (("values", stages[2]), ("sums", stages[1]), ("logits", stages[0]),
                                    ("weights", stages[1]), ("proj", more)):
                    after.get(phase, nothing)(f, part)
                if n == SB_HEADS:
                    after.get("gate units", nothing)(f, 0)
            at += batches
            before.get("prime", nothing)(f)
            step("gates", at, at % 2, 0)
            step("out", at + 1, (at + 1) % 2, 0)
            at += 2
            with chain.loop(TURN_G - 1, links["gates"] + 2 * per) as i:
                before.get("gate units", nothing)(f, 1 + i)
                step("gates", at + 2 * i, at % 2, 1 + i)
                step("out", at + 1 + 2 * i, (at + 1) % 2, 1 + i)
            if f < 2:
                before.get("norm", nothing)(f)
                after.get("norm", nothing)(f)
            else:
                step("norm", 19, 1)
            if peer:
                with chain.loop(2, 4 * (links["topk"] + per)) as i:
                    for s in range(4):
                        step("topk", 20 + 4 * i + s, s % 2, 4 * i + s, s, i)
            else:
                for h in range(HEADS):
                    if h == HEADS - 2:
                        before.get("head", nothing)(1)
                    if h == HEADS - 1:
                        after.get("head", nothing)(1)
                    b = h - FIRST_AT
                    if b == 0:
                        before.get("start", nothing)(0)
                    before.get("topk", nothing)(0, h, h % 4, h // 4)
                    if 0 <= b < EARLY:
                        batch(0, b, b % 2)
                    after.get("topk", nothing)(0, h, h % 4, h // 4)

        def tail(chain, j, batch, links):
            first = {0: NBATCH, TILES - 1: 0}.get(j, WOVEN)
            if first < NBATCH:
                with chain.loop((NBATCH - first) // 2, 2 * links["batch"]) as i:
                    for u in range(2):
                        batch(j, first + 2 * i + u, u)

        def program(chain, batch, before, after, links):
            weave(chain, 0, batch, before, after, links)
            for j in range(TILES):
                if j > 0:
                    before.get("start", nothing)(j)
                if j < TILES - 1:
                    weave(chain, j + 1, batch, before, after, links)
                tail(chain, j, batch, links)
                after.get("tile", nothing)(j)

        block = ctx.enter_context(nc.Block())

        @block.sync
        def _(sp_q):
            sp_q.dma_start(hT[:, :, PAD:2 * P], xT[:, :, 0:P + META]).then_inc(x_in, 16)
            sp_q.dma_start(g1_sb[:], g1).then_inc(taps_in, 16)
            sp_q.dma_start(cw_sb[:], cw).then_inc(taps_in, 16)
            for s in range(WR):
                sp_q.dma_start(wring[:, s, :], weights[s]).then_inc(w_in[s], 16)
            sp_q.dma_start(g2_b[:], g2.partition_broadcast(P)).then_inc(s_const, 16)
            sp_q.dma_start(gf_b[:], gf.partition_broadcast(P)).then_inc(s_const, 16)
            sp_q.dma_start(sk_sb[:], sk).then_inc(s_const, 16)

            def turn(unit, free):
                for s, (done, count) in enumerate(free):
                    sp_q.wait_ge(done, count)
                    src = weights[unit + s] if isinstance(unit, int) else \
                        weights[bass.ds(unit + s, 1)].rearrange("o p n -> (o p) n")
                    sp_q.dma_start(wring[:, s, :], src).then_inc(w_in[s], 16)

            for f in range(TILES):
                heads = [(q_mm, HEADS * f - WR + s + 1) for s in range(WR)]
                if f < 2:
                    if f > 0:
                        turn(0, heads)
                    with sp_q.Fori(1, TURN_C) as t:
                        turn(WR * t, [(c_mm, UNIT_C * f - WR + s + 1 + t * WR) for s in range(WR)])
                    turn(UNIT_C, [(c_mm, UNIT_C * f + UNIT_C - WR + s + 1) for s in range(WR)])
                else:
                    turn(UNIT_C, heads)
                with sp_q.Fori(1, TURN_G + 1) as t:
                    n = t + 4 * f
                    turn(UNIT_C + WR * t, [(gate_mm, n), (gate_mm, n), (br_mm, 2 * n), (x1_mm, n)])
                turn(UNIT_C + UNIT_G + WR, [(q_mm, HEADS * f + s + 1) for s in range(WR)])

        @block.gpsimd
        def _(pool):
            pool.wait_ge(s_fill, 1)
            nc.gpsimd.affine_select(out=ident[:], in_=ones[:], compare_op=ALU.is_equal, fill=0.0, base=0,
                                    pattern=[[-1, P]], channel_multiplier=1)
            nc.gpsimd.affine_select(out=neg_tri[:], in_=neg_ones[:], compare_op=ALU.is_ge, fill=0.0, base=0,
                                    pattern=[[-1, P]], channel_multiplier=1)
            nc.gpsimd.affine_select(out=past[:], in_=ones[:], compare_op=ALU.is_gt, fill=0.0, base=0,
                                    pattern=[[1, P]], channel_multiplier=-1)
            nc.gpsimd.iota(iota16[:], pattern=[[1, TOPK]], base=0, channel_multiplier=0,
                           allow_small_or_imprecise_dtypes=True).then_inc(s_masks, 1)

            def gather(j, b, u):
                n = NBATCH * j + b
                for s in range(BATCH):
                    slot = BATCH * u + s
                    if not (isinstance(n, int) and n < 2):
                        pool.wait_ge(v_done, BATCH * n - RING + s + 1)
                        pool.nop(nofuse=True)
                    nc.gpsimd.tensor_copy(stage_idx[:, u, s:s + 1], idx[:, j % 2, bass.ds(BATCH * b + s, 1)]).then_inc(st_idx, 1)
                    pool.wait_ge(st_idx, BATCH * n + s + 1)
                    pool.nop(nofuse=True)
                    nc.gpsimd.indirect_dma_start(
                        out=rows[:, slot, :], out_offset=None, in_=table,
                        in_offset=bass.IndirectOffsetOnAxis(ap=stage_idx[:, u, s:s + 1], axis=0),
                    ).then_inc(row_in[slot], 16)

            per_head = TOPK // BATCH

            def head_rows(j, h):
                pool.wait_ge(idx_ready, HEADS * j + h + 1)
                for b in range(per_head):
                    gather(j, per_head * h + b, b % 2)

            for j in range(TILES):
                if j == 0:
                    head_rows(0, 0)
                with pool.Fori(1 if j == 0 else 0, HEADS) as h:
                    head_rows(j, h)

        @block.scalar
        def _(eng):
            chain = Chain(eng, act_self)
            link = chain.link

            def activation(*a, **k):
                return nc.scalar.activation(*a, **k)

            def copy(o, i):
                return activation(o, i, ACT.Copy)

            def rsqrt_mean(dst, tmp, src):
                link(activation(tmp, src, ACT.Ln, scale=1.0 / D, bias=eps[:]))
                return activation(dst, tmp, ACT.Exp, scale=-0.5)

            def square(g):
                n = width(g)
                if g == 0:
                    eng.wait_ge(s_fill, 2)
                eng.wait_ge(x_in, 16 * (g + 1))
                for r in range(4):
                    if r >= 2:
                        eng.wait_ge(ssum_mm, 4 * g + r - 1)
                    dst = (h2 if r % 2 else x1)[:, 1, 0:2 * n].rearrange("p (c n) -> p c n", c=2)
                    activation(dst, hT[:, 2 * r:2 * r + 2, lo(g):lo(g) + n], ACT.Square).then_inc(sq_ready, 1)

            def head_scale(g):
                n = width(g)
                eng.wait_ge(ssum_mm, 4 * (g + 1))
                rsqrt_mean(rstd[:, 0:n], rstd[:, 0:n], pf[:, 0, 0:n]).then_inc(rstd_ready, 1)
                load_residual(g)

            def load_residual(f):
                if f >= 2:
                    eng.wait_ge(out_stored, 16 * (f - 1))
                eng.dma_start(x1[:, f % 2, :], x[P * f:P * (f + 1), :]).then_inc(res_in, 16)

            def proj(g, units):
                for u in units:
                    proj_unit(g, u)

            def proj_unit(g, u):
                n, t = width(g), tokens(g)
                bank = two_banks(u)
                new = bank[:, :, 0:n]
                eng.wait_ge(c_mm, UNIT_C * g + u + 1)
                if u < 2:
                    at = PAD if g == 0 else 2 * P
                    ins = copy(kT[:, 2 * u:2 * u + 2, at:at + n], new)
                elif u < 4:
                    cols = slice(256 * (u - 2), 256 * (u - 2) + 256)
                    pair = bank[:, 0, :].rearrange("p (t n) -> p t n", t=2)
                    if g == 0:
                        ins = copy(v[:, 0:2, cols], pair)
                    else:
                        copy(v[:, 2:4, cols], pair)
                        ins = copy(v[:, 4, cols], bank[:, 1, 0:256])
                elif u < 6:
                    ins = activation(qT[:, 2 * (u - 4):2 * (u - 4) + 2, 0:t], bank[:, :, n - t:n], ACT.Copy, scale=0.125)
                else:
                    if u < 8 and g > 0:
                        eng.wait_ge(conv_done, 2 * g)
                    elif u >= 8:
                        eng.wait_ge(cs_used, 4 * g + u - 7)
                    ins = copy(cs[:, u % 2, :, 0:n], new)
                ins.then_inc(c_ev, 1)

            def attn(f, heads):
                nk = f + 2
                if f >= 2 and 0 in heads:
                    load_residual(f)
                for h in heads:
                    s = sp[:, h % 2, 0:nk * P]
                    eng.wait_ge(z_mm, SB_HEADS * f + h + 1)
                    link(activation(s, logit_banks(f, h)[:, 0:nk * P], ACT.Abs))
                    link(activation(s, s, ACT.Exp, scale=-1.0))
                    activation(s, s, ACT.Ln, bias=1.0).then_inc(ln_ready, 1)

            def weights_of(f, heads):
                nk = f + 2
                for h in heads:
                    e = h % 2
                    last = sp[:, e, (nk - 1) * P:nk * P]
                    eng.wait_ge(mn_ready, SB_HEADS * f + h + 1)
                    activation(sp[:, e, 0:(nk - 1) * P], logit_banks(f, h)[:, 0:(nk - 1) * P], ACT.Exp)
                    activation(last, last, ACT.Exp).then_inc(ex_ready, 1)

            def attended(f, heads):
                for h in heads:
                    r = slice(64 * (h % 2), 64 * (h % 2) + 64)
                    eng.wait_ge(o_mm, SB_HEADS * f + h + 1)
                    copy(oT[r, h // 2, :], px[r, 0:P]).then_inc(o_ev, 1)

            def gates(f, d):
                eng.wait_ge(gate_mm, 4 * f + d + 1)
                link(activation(sg[:], pf[:, 0, :], ACT.Exp, scale=-1.0))
                link(activation(sg[:], sg[:], ACT.Ln, bias=1.0))
                activation(sg[:], sg[:], ACT.Exp, scale=-1.0).then_inc(ge_ready, 1)

            def norm(f):
                eng.wait_ge(x1_mm, 4 * (f + 1))
                link(activation(h2[:, f % 2, :], px[:], ACT.Square, accum_out=ss2[:, 0:1]))
                rsqrt_mean(rs2[:, 0:1], ss2[:, 0:1], ss2[:, 0:1]).then_inc(rs2_ready, 1)
                eng.wait_ge(h2_ready, f + 1)
                copy(x1[:, f % 2, :], px[:])
                if f == 0:
                    at = META + P
                    eng.dma_start(hT[:], xT[:, :, at:at + GROUP]).then_inc(x_in, 16)

            def transposed(f):
                eng.wait_ge(tr_mm, f + 1)
                eng.wait_ge(conv_done, 2 * min(f + 1, 2))
                copy(h2T, pf[:, 0:2, :].rearrange("p b (c n) -> p (b c) n", n=P)).then_inc(h2T_ready, 1)

            def query(f, h, s, i):
                eng.wait_ge(q_mm, HEADS * f + h + 1)
                copy(qh[:], pf[:, 2, 0:256]).then_inc(qh_ready, 1)

            def softmax(f, h, s, i):
                n = HEADS * f + h + 1
                eng.wait_ge(nm_ready, n)
                activation(esc[:], score[:], ACT.Exp, bias=nmax[:], accum_out=esum[:, 0:1]).then_inc(es_ready, 1)

            def batch(j, b, u):
                n = NBATCH * j + b
                eng.wait_ge(arg_ready, n + 1)
                activation(g_exp[:, u, :], g_arg[:, u, :], ACT.Exp, scale=-GELU_B).then_inc(gexp_ready, 1)
                eng.wait_ge(coef_ready, n + 1)
                if not (isinstance(n, int) and n < 2):
                    eng.wait_ge(v_done, BATCH * n - BATCH)
                for s in range(BATCH - by_dve(n)):
                    activation(diag[:, BATCH * u + s, :], ident[:], ACT.Copy,
                               scale=coef[:, u, s:s + 1]).then_inc(diag_ready, 1)

            def end_tile(j):
                eng.wait_ge(v_done, SEL * (j + 1))
                link(activation(h2[:, j % 2, :], py[:], ACT.Square, accum_out=ss2[:, 1:2]))
                rsqrt_mean(rs2[:, 1:2], ss2[:, 1:2], ss2[:, 1:2]).then_inc(rs3_ready, 1)
                eng.wait_ge(out_ready, j + 1)
                eng.dma_start(out[P * j:P * (j + 1), :], x1[:, j % 2, :]).then_inc(out_stored, 16)

            nc.scalar.preload_act_table_set("natural_log_exp_and_others")
            eng.wait_ge(s_masks, 1)
            program(chain, batch,
                    before={"head": square, "norm": norm, "topk": query},
                    after={"head": head_scale, "proj": proj, "logits": attn, "weights": weights_of,
                           "values": attended, "gates": gates, "norm": transposed, "topk": softmax, "tile": end_tile},
                    links={"batch": 0, "gates": 2, "topk": 0})
            eng.wait_ge(out_stored, 16 * TILES)

        @block.vector
        def _(eng):
            chain = Chain(eng, dve_self)
            link = chain.link
            dve = nc.vector

            def head(g):
                n = width(g)
                eng.wait_ge(rstd_ready, g + 1)
                for c in range(DC):
                    h = hT[:, c, lo(g):lo(g) + n]
                    dve.scalar_tensor_tensor(out=h, in0=h, scalar=g1_sb[:, c:c + 1], in1=rstd[:, 0:n],
                                             op0=ALU.mult, op1=ALU.mult).then_inc(h_ready, 1)

            def proj(g, units):
                for u in units:
                    if 6 <= u < 10:
                        convolve(g, u, u - 6)
                    elif u >= 10:
                        times_b(g, u, 2 * (u - 10))

            def convolve(g, u, i):
                n, t = width(g), tokens(g)
                off = n - t
                eng.wait_ge(c_ev, UNIT_C * g + u + 1)
                dve.tensor_copy(cu[:, 0:2], carry[:, i, :])
                dve.tensor_tensor(cu[:, 2:2 + n], cs[:, u % 2, 0, 0:n], cs[:, u % 2, 1, 0:n], ALU.mult).then_inc(cs_used, 1)
                eng.wait_ge(cs_used, 4 * g + i + 1)
                y = yaT[:, i, 0:t]
                dve.tensor_copy(carry[:, i, :], cu[:, n:n + 2])
                link(dve.tensor_scalar(y, cu[:, off:off + t], cw_sb[:, i, 0:1], None, ALU.mult))
                for k in range(1, 3):
                    link(dve.scalar_tensor_tensor(out=y, in0=cu[:, off + k:off + k + t], scalar=cw_sb[:, i, k:k + 1],
                                                  in1=y, op0=ALU.mult, op1=ALU.add))

            def times_b(g, u, i):
                n, t = width(g), tokens(g)
                eng.wait_ge(c_ev, UNIT_C * g + u + 1)
                y = yaT[:, i:i + 2, 0:t]
                dve.tensor_tensor(y, y, cs[:, u % 2, :, n - t:n], ALU.mult).then_inc(conv_done, 1)

            def attn(f, heads):
                nk = f + 2
                for h in heads:
                    s = sp[:, h % 2, 0:nk * P]
                    eng.wait_ge(ln_ready, SB_HEADS * f + h + 1)
                    link(dve.scalar_tensor_tensor(out=s, in0=logit_banks(f, h)[:, 0:nk * P], scalar=0.0, in1=s,
                                                  op0=ALU.max, op1=ALU.add))
                    dve.tensor_tensor(diagonal(f, h), diagonal(f, h), past[:], ALU.mult).then_inc(sp_ready, 1)

            def diagonal(f, h):
                return sp[:, h % 2, (f + 1) * P:(f + 2) * P]

            def sums(f, heads):
                for h in heads:
                    eng.wait_ge(tri_mm, SB_HEADS * f + h + 1)
                    dve.tensor_scalar(diagonal(f, h), logit_banks(f, h)[:, (f + 1) * P:(f + 2) * P], 0.0, None,
                                      ALU.min).then_inc(mn_ready, 1)

            def weights_of(f, heads):
                for h in heads:
                    eng.wait_ge(ex_ready, SB_HEADS * f + h + 1)
                    dve.tensor_tensor(diagonal(f, h), diagonal(f, h), past[:], ALU.mult).then_inc(at_ready, 1)

            def gates(f, d):
                n = 4 * f + d + 1
                eng.wait_ge(ge_ready, n)
                for k in range(2):
                    eng.wait_ge(br_mm, 2 * n - 1 + k)
                    s = sg[:, 2 * P * k:2 * P * (k + 1)]
                    link(dve.tensor_tensor(s, s, pf[:, 1 + k, 0:2 * P], ALU.mult))
                    dve.tensor_tensor(mixT[:, k, :], s[:, 0:P], s[:, P:2 * P], ALU.add).then_inc(mix_ready, 1)

            def norm(f):
                eng.wait_ge(rs2_ready, f + 1)
                if f == 0:
                    eng.wait_ge(s_const, 16 * 3)
                dve.scalar_tensor_tensor(out=h2[:, f % 2, :], in0=px[:], scalar=rs2[:, 0:1], in1=g2_b[:],
                                         op0=ALU.mult, op1=ALU.mult).then_inc(h2_ready, 1)

            def topk(f, h, s, i):
                n = HEADS * f + h + 1
                eng.wait_ge(sc_mm, n)
                eng.nop(nofuse=True)
                sc = pf[:, 3, 0:256].rearrange("p (t n) -> p t n", t=2)
                dve.max(tops[:, 0, 0:8], sc[:, 0, :])
                link(dve.max(tops[:, 1, 0:8], sc[:, 1, :]))
                eng.nop(nofuse=True)
                for t in range(2):
                    dve.max_index(topi[:, t, 0:8], tops[:, t, 0:8], sc[:, t, :])
                for t in range(2):
                    ins = dve.match_replace(rest[:, t, :], tops[:, t, 0:8], sc[:, t, :], NEG)
                ins.then_inc(sc_used, 1)
                eng.wait_ge(sc_used, n)
                eng.nop(nofuse=True)
                dve.max(tops[:, 0, 8:16], rest[:, 0, :])
                link(dve.max(tops[:, 1, 8:16], rest[:, 1, :]))
                eng.nop(nofuse=True)
                for t in range(2):
                    dve.max_index(topi[:, t, 8:16], tops[:, t, 8:16], rest[:, t, :])
                link(dve.tensor_tensor(cand[:].rearrange("p (a b) -> p a b", a=TOPK),
                                       tops[:, 0, :].unsqueeze(2).broadcast_to([P, TOPK, TOPK]),
                                       tops[:, 1, :].unsqueeze(1).broadcast_to([P, TOPK, TOPK]), ALU.add))
                dve.tensor_copy(topf[:], topi[:])
                link(dve.max(score[:, 0:8], cand[:]))
                dve.tensor_scalar(nmax[:], score[:, 0:1], -1.0, None, ALU.mult)
                dve.max_index(ci[:, 0:8], score[:, 0:8], cand[:])
                link(dve.match_replace(cand2[:], score[:, 0:8], cand[:], NEG))
                eng.nop(nofuse=True)
                dve.max(score[:, 8:16], cand2[:]).then_inc(nm_ready, 1)
                eng.wait_ge(nm_ready, n)
                eng.nop(nofuse=True)
                link(dve.max_index(ci[:, 8:16], score[:, 8:16], cand2[:]))
                dve.tensor_scalar(cab[:, 0, :], ci[:], 4, None, ALU.logical_shift_right)
                link(dve.tensor_scalar(cab[:, 1, :], ci[:], TOPK - 1, None, ALU.bitwise_and))
                link(dve.tensor_tensor(hit[:].rearrange("p t k j -> p (t k) j"),
                                       cab[:].rearrange("p t k -> p (t k)").unsqueeze(2).broadcast_to([P, 2 * TOPK, TOPK]),
                                       iota16[:].unsqueeze(1).broadcast_to([P, 2 * TOPK, TOPK]), ALU.is_equal))
                for t in range(2):
                    ins = dve.tensor_tensor(hit[:, t], hit[:, t], topf[:, t, :].unsqueeze(1).broadcast_to([P, TOPK, TOPK]), ALU.mult)
                link(ins)
                link(dve.tensor_reduce(picked[:], hit[:], AX_X, ALU.add))
                eng.wait_ge(es_ready, n)
                link(dve.reciprocal(esum[:, 1:2], esum[:, 0:1]))
                dve.tensor_scalar(gate[:, f % 2, bass.ds(TOPK * h, TOPK)], esc[:], esum[:, 1:2], None, ALU.mult)
                dve.scalar_tensor_tensor(out=idx[:, f % 2, bass.ds(TOPK * h, TOPK)], in0=picked[:, 0, :], scalar=128.0,
                                         in1=picked[:, 1, :], op0=ALU.mult, op1=ALU.add).then_inc(idx_ready, 1)

            def batch(j, b, u):
                n = NBATCH * j + b
                turn = (NBATCH // 2) * j + (b - u) // 2 if isinstance(b, int) else None
                for s in range(BATCH):
                    slot = BATCH * u + s
                    eng.wait_ge(row_in[slot], 16 * (turn + 1) if turn is not None else 8 * (n - u) + 16)
                    ins = dve.tensor_tensor_reduce(out=rows[:, slot, 0:D], in0=rows[:, slot, 0:D], in1=h2[:, j % 2, :],
                                                   scale=1.0, scalar=0.0, op0=ALU.mult, op1=ALU.add,
                                                   accum_out=act[:, u, s:s + 1])
                link(ins)
                a, arg, co = act[:, u, :], g_arg[:, u, :], coef[:, u, :]
                dve.tensor_tensor(co, a, gate[:, j % 2, bass.ds(BATCH * b, BATCH)], ALU.mult)
                link(dve.tensor_tensor(arg, a, a, ALU.mult))
                link(dve.tensor_scalar(arg, arg, GELU_A, 1.0, ALU.mult, ALU.add))
                dve.tensor_tensor(arg, arg, a, ALU.mult).then_inc(arg_ready, 1)
                eng.wait_ge(gexp_ready, n + 1)
                link(dve.tensor_scalar(a, g_exp[:, u, :], 1.0, None, ALU.add))
                link(dve.reciprocal(a, a))
                dve.tensor_tensor(co, co, a, ALU.mult).then_inc(coef_ready, 1)
                for i in range(by_dve(n)):
                    s, k = BATCH - by_dve(n) + i, by_dve_before(n) + i
                    row = rows[:, BATCH * u + s, D:2 * D]
                    if i == 0:
                        eng.wait_ge(coef_ready, n + 1)
                    if k == 0:
                        dve.tensor_scalar(acc, row, coef[:, u, s:s + 1], None, ALU.mult).then_inc(acc_done, 1)
                    else:
                        eng.wait_ge(acc_done, k)
                        dve.scalar_tensor_tensor(out=acc, in0=row, scalar=coef[:, u, s:s + 1], in1=acc,
                                                 op0=ALU.mult, op1=ALU.add).then_inc(acc_done, 1)

            def end_tile(j):
                eng.wait_ge(rs3_ready, j + 1)
                dve.scalar_tensor_tensor(out=x1[:, j % 2, :], in0=py[:], scalar=rs2[:, 1:2], in1=gf_b[:],
                                         op0=ALU.mult, op1=ALU.mult).then_inc(out_ready, 1)

            dve.memset(neg_ones[:], -1.0)
            dve.memset(ones[:], 1.0).then_inc(s_fill, 1)
            dve.memset(eps[:], EPS)
            dve.memset(hT[:, :, 0:PAD], 0.0)
            dve.memset(kT[:, :, 0:PAD], 0.0)
            dve.memset(carry[:], 0.0).then_inc(s_fill, 1)
            eng.wait_ge(s_fill, 2)
            eng.wait_ge(s_masks, 1)
            eng.wait_ge(taps_in, 16 * 2)
            program(chain, batch,
                    before={"norm": norm},
                    after={"head": head, "proj": proj, "logits": attn, "sums": sums, "weights": weights_of,
                           "gates": gates, "topk": topk, "tile": end_tile},
                    links={"batch": 5, "gates": 2, "topk": 11})

        @block.tensor
        def _(eng):
            chain = Chain(eng, None)
            mm = nc.tensor.matmul

            def weight(slot, turn):
                eng.wait_ge(w_in[slot], 16 * (turn + 1))

            def head(g):
                n = width(g)
                for r in range(4):
                    eng.wait_ge(sq_ready, 4 * g + r + 1)
                    for c in range(2):
                        ins = mm(pf[:, 0, 0:n], ones[:], (h2 if r % 2 else x1)[:, 1, c * n:(c + 1) * n],
                                 start=(r == 0 and c == 0), stop=(r == 3 and c == 1))
                    ins.then_inc(ssum_mm, 1)

            def proj(g, units):
                for u in units:
                    proj_unit(g, u)

            def proj_unit(g, u):
                n = width(g)
                slot = u % WR
                w = w_unit[slot]
                if u == 0:
                    if g > 0:
                        eng.wait_ge(sc_used, HEADS)
                if u >= 2:
                    eng.wait_ge(c_ev, UNIT_C * g + (u if u > 6 else u - 1))
                weight(slot, first_turn(g) + u // WR)
                if u in (2, 3):
                    for t in range(2 if g == 0 else 3):
                        for c in range(DC):
                            ins = mm(two_banks(u)[:, t // 2, 256 * (t % 2):256 * (t % 2) + 256],
                                     hT[:, c, P * t:P * t + P], w[:, c, :], start=(c == 0), stop=(c == DC - 1))
                else:
                    for half in range(2):
                        for c in range(DC):
                            if u == 0 and half == 0:
                                eng.wait_ge(h_ready, DC * g + c + 1)
                            ins = mm(two_banks(u)[:, half, 0:n], w[:, c, half * P:(half + 1) * P],
                                     hT[:, c, lo(g):lo(g) + n], start=(c == 0), stop=(c == DC - 1))
                ins.then_inc(c_mm, 1)

            def logits(f, heads):
                nk = f + 2
                for h in heads:
                    e = h % 2
                    r = slice(64 * e, 64 * e + 64)
                    if h < 2:
                        eng.wait_ge(c_ev, 6 + UNIT_C * min(f, 1))
                    for m in range(nk):
                        ins = mm(logit_banks(f, h)[:, m * P:(m + 1) * P], kT[r, h // 2, m * P:(m + 1) * P],
                                 qT[r, h // 2, col(f):col(f) + P],
                                 start=(m % 4 == 0), stop=False, skip_group_check=True)
                    ins.then_inc(z_mm, 1)

            def attn(f, heads):
                nk = f + 2
                for h in heads:
                    e = h % 2
                    eng.wait_ge(sp_ready, SB_HEADS * f + h + 1)
                    for m in range(nk):
                        mm(logit_banks(f, h)[:, m * P:(m + 1) * P], neg_tri[:], sp[:, e, m * P:(m + 1) * P],
                           start=False, stop=False, skip_group_check=True)
                    for m in range(1, nk):
                        src = sp[:, e, m * P:(m + 1) * P].unsqueeze(1).broadcast_to([P, m, P])
                        ins = mm(logit_banks(f, h)[:, 0:m * P].rearrange("p (m n) -> p m n", n=P), neg_ones[:], src,
                                 start=False, stop=True, skip_group_check=True)
                    ins.then_inc(tri_mm, 1)

            def values(f, heads):
                nk = f + 2
                for h in heads:
                    e = h % 2
                    r = slice(64 * e, 64 * e + 64)
                    if h >= 2:
                        eng.wait_ge(o_ev, SB_HEADS * f + h - 1)
                    eng.wait_ge(at_ready, SB_HEADS * f + h + 1)
                    for m in range(nk):
                        ins = mm(px[r, 0:P], v[:, m, 64 * h:64 * h + 64], sp[:, e, m * P:(m + 1) * P],
                                 start=(m == 0), stop=(m == nk - 1))
                    ins.then_inc(o_mm, 1)

            def prime(f):
                if f == 1:
                    eng.wait_ge(acc_done, sum(BY_DVE.values()))
                    for half in range(2):
                        mm(py[:, 512 * half:512 * half + 512], ident[:], acc[:, 512 * half:512 * half + 512],
                           start=False, stop=False, skip_group_check=True)
                eng.wait_ge(res_in, 16 * (f + 1))
                eng.wait_ge(o_ev, SB_HEADS * (f + 1))
                eng.wait_ge(conv_done, 2 * min(f + 1, 2))
                for half in range(2):
                    mm(px[:, 512 * half:512 * half + 512], ident[:], x1[:, f % 2, 512 * half:512 * half + 512],
                       start=True, stop=False, skip_group_check=True)

            def gate_units(f, d):
                if isinstance(d, int) and f < 2:
                    eng.wait_ge(c_ev, UNIT_C * (f + 1))
                for k in range(2):
                    weight(k, gate_turn(f) + d)
                    for half in range(2):
                        for c in range(DC):
                            ins = mm(pf[:, 0, (2 * k + half) * P:(2 * k + half + 1) * P],
                                     w_unit[k][:, c, half * P:(half + 1) * P], h_tile(f)[:, c, :],
                                     start=(c == 0), stop=(c == DC - 1))
                ins.then_inc(gate_mm, 1)

            def branches(f, d):
                weight(2, gate_turn(f) + d)
                for k in range(2):
                    for g, src in enumerate((yaT[:, :, col(f):col(f) + P], oT)):
                        for c in range(CC):
                            ins = mm(pf[:, 1 + k, g * P:(g + 1) * P],
                                     w_unit[2][:, CC * g + c, k * P:(k + 1) * P], src[:, c, :],
                                     start=(c == 0), stop=(c == CC - 1))
                    ins.then_inc(br_mm, 1)

            def out_product(f, d):
                n = 4 * f + d + 1
                weight(3, gate_turn(f) + d)
                for k in range(2):
                    eng.wait_ge(mix_ready, 2 * n - 1 + k)
                    for half in range(2):
                        ins = mm(px[:, 512 * half:512 * half + 512], mixT[:, k, :],
                                 w_out_unit[:, k, 512 * half:512 * half + 512],
                                 start=False, stop=False, skip_group_check=True)
                ins.then_inc(x1_mm, 1)

            def norm(f):
                eng.wait_ge(h2_ready, f + 1)
                for c in range(DC):
                    ins = nc.tensor.transpose(pf[:, c // 4, (c % 4) * P:(c % 4 + 1) * P], h2[:, f % 2, c * P:(c + 1) * P], ident[:])
                ins.then_inc(tr_mm, 1)

            def topk(f, h, s, i):
                n = HEADS * f + h + 1
                eng.wait_ge(h2T_ready, f + 1)
                weight(s, gate_turn(f) + TURN_G + i)
                for t in range(2):
                    for c in range(DC):
                        ins = mm(pf[:, 2, t * P:(t + 1) * P], w_unit[s][:, c, t * P:(t + 1) * P], h2T[:, c, :],
                                 start=(c == 0), stop=(c == DC - 1))
                ins.then_inc(q_mm, 1)
                eng.wait_ge(qh_ready, n)
                if isinstance(h, int) and h == 0:
                    eng.wait_ge(s_const, 16 * 3)
                else:
                    eng.wait_ge(sc_used, n - 1)
                for t in range(2):
                    ins = mm(pf[:, 3, t * P:(t + 1) * P], qh[:, t * P:(t + 1) * P],
                             sk_sb[:, bass.ds(2 * h + t, 1), :].rearrange("p o n -> p (o n)"), start=True, stop=True)
                ins.then_inc(sc_mm, 1)

            def start_tile(j):
                eng.wait_ge(h2T_ready, j + 1)
                if j > 0:
                    eng.wait_ge(out_ready, j)
                for half in range(2):
                    mm(py[:, 512 * half:512 * half + 512], ident[:], x1[:, j % 2, 512 * half:512 * half + 512],
                       start=True, stop=False, skip_group_check=True)

            def batch(j, b, u):
                n = NBATCH * j + b
                for s in range(BATCH - by_dve(n)):
                    eng.wait_ge(diag_ready, BATCH * n - by_dve_before(n) + s + 1)
                    for half in range(2):
                        ins = mm(py[:, 512 * half:512 * half + 512], diag[:, BATCH * u + s, :],
                                 rows[:, BATCH * u + s, D + 512 * half:D + 512 * half + 512],
                                 start=False, stop=False, skip_group_check=True)
                    ins.then_inc(v_done, 1)
                for i in range(by_dve(n)):
                    eng.wait_ge(acc_done, by_dve_before(n) + i + 1)
                    mm(px[:, D - 1:D], ident[:], ones[:, 0:1], start=True, stop=True).then_inc(v_done, 1)

            eng.wait_ge(s_masks, 1)
            eng.wait_ge(s_fill, 2)
            program(chain, batch,
                    before={"head": head, "proj": proj, "logits": logits, "values": values, "prime": prime,
                            "gate units": gate_units, "gates": branches, "out": out_product, "topk": topk, "start": start_tile},
                    after={"logits": attn, "gate units": gate_units, "norm": norm},
                    links={"batch": 0, "gates": 0, "topk": 0})


def weight_units(np, w_in, w_branch_a, w_branch_b, w_out, w_q):
    def unit(w, *cols):
        return np.concatenate([w[:, a:b].reshape(-1, P, b - a) for a, b in cols], axis=2).transpose(1, 0, 2)

    def halves(at):
        return [unit(w_in, (at + 256 * i, at + 256 * i + 256)) for i in range(2)]

    units = halves(2048) + halves(2560) + halves(1536)
    units += [unit(w_in, (512 + P * i, 640 + P * i), (1024 + P * i, 1152 + P * i)) for i in range(4)]
    units += halves(0)
    for d in range(4):
        for k in range(2):
            at = P * (2 * d + k)
            units.append(unit(w_in, (3072 + at, 3072 + at + P), (4096 + at, 4096 + at + P)))
        cols = (256 * d, 256 * d + 256)
        units.append(np.concatenate([unit(w_branch_a, cols), unit(w_branch_b, cols)], axis=1))
        units.append(w_out[256 * d:256 * d + 256].reshape(2, P, D).transpose(1, 0, 2))
    units += [unit(w_q, (256 * h, 256 * h + 256)) for h in range(HEADS)]
    return np.ascontiguousarray(np.stack([u.reshape(P, 2048) for u in units]))


def kernel(**inputs):
    import numpy as np
    import concourse.bacc as bacc
    from concourse.bass_utils import run_bass_kernel_spmd

    a = {k: np.asarray(t) for k, t in inputs.items()}
    x = a["x"][0]
    tokens = np.concatenate([a["meta"], x], axis=0)
    arrays = {
        "xT": np.ascontiguousarray(tokens.T.reshape(DC, P, META + SEQ).transpose(1, 0, 2)),
        "x": np.ascontiguousarray(x),
        "g1": np.ascontiguousarray(a["norm1_g"].reshape(DC, P).T),
        "cw": np.ascontiguousarray(a["conv_w"].reshape(3, CC, P).transpose(2, 1, 0)),
        "g2": a["norm2_g"],
        "gf": a["final_g"],
        "sk": np.ascontiguousarray(a["peer_subkeys"].reshape(2 * HEADS, P, P).transpose(2, 0, 1)),
        "weights": weight_units(np, a["w_in"], a["w_branch_a"], a["w_branch_b"], a["w_out"], a["peer_w_q"]),
        "table": np.concatenate([a["peer_u"], a["peer_v"]], axis=1),
    }
    nc = bacc.Bacc("TRN2", target_bir_lowering=False, num_devices=1)
    aps = [nc.dram_tensor(k, t.shape, F32, kind="ExternalInput").ap() for k, t in arrays.items()]
    out = nc.dram_tensor("out", (SEQ, D), F32, kind="ExternalOutput").ap()
    hybrid_block(nc, *aps, out)
    r = run_bass_kernel_spmd(nc, [arrays], core_ids=[0])
    return r.results[0]["out"].reshape(1, SEQ, D)
```
